# Optimizing a Trainium2 kernel written in Bass

```python
import math
import jax, jax.numpy as jnp
from jax import lax
import numpy as np

D_MODEL = 1024
BATCH = 1
SEQ = 256
DEPTH = 4

CHUNK = 64
N_MIXERS = 3
EPS = 1e-6
D_FF = 4 * D_MODEL
MEM_LEN = 256
X_HEADS = 4
X_HEAD_DIM = 256
X_WIDTH = X_HEADS * X_HEAD_DIM
SSM_D_INNER = 2 * D_MODEL
SSM_HEAD_DIM = 64
SSM_HEADS = SSM_D_INNER // SSM_HEAD_DIM
SSM_GROUPS = 8
SSM_HPG = SSM_HEADS // SSM_GROUPS
SSM_STATE = 128
SSM_CONV = 4
SSM_BC = SSM_GROUPS * SSM_STATE
SSM_CONV_DIM = SSM_D_INNER + 2 * SSM_BC
SSM_IN = SSM_D_INNER + SSM_CONV_DIM + SSM_HEADS + X_WIDTH
DIFF_HEADS = 8
DIFF_HEAD_DIM = 64
DIFF_V_DIM = 2 * DIFF_HEAD_DIM
DIFF_QK = DIFF_HEADS * 2 * DIFF_HEAD_DIM
DIFF_WIDTH = DIFF_HEADS * DIFF_V_DIM
DIFF_IN = 2 * DIFF_QK + DIFF_WIDTH + X_WIDTH
Q_BLOCK = 128
SGU_BLOCK = 128
SGU_GROUPS = 8
SGU_WIDTH = D_MODEL
SGU_GROUP_DIM = SGU_WIDTH // SGU_GROUPS
SGU_IN = 2 * SGU_WIDTH + X_WIDTH
N_SSM = (DEPTH + 2) // 3
N_DIFF = (DEPTH + 1) // 3
N_SGU = DEPTH // 3

kernel_name = 'hybrid_streaming_encoder_trunk'

def rmsnorm(x, g):
    xf = x.astype(jnp.float32)
    y = xf * lax.rsqrt(jnp.mean(xf * xf, axis=-1, keepdims=True) + EPS)
    return (y * g.astype(jnp.float32)).astype(x.dtype)

def memory_cross_attention(q, mem_n, w_kv, gq, gk):
    b, l, _ = q.shape
    m = mem_n.shape[1]
    k, v = jnp.split(mem_n @ w_kv, 2, axis=-1)
    q = rmsnorm(q.reshape(b, l, X_HEADS, X_HEAD_DIM), gq)
    k = rmsnorm(k.reshape(b, m, X_HEADS, X_HEAD_DIM), gk)
    v = v.reshape(b, m, X_HEADS, X_HEAD_DIM)
    s = jnp.einsum('blhd,bmhd->bhlm', q, k).astype(jnp.float32) * (X_HEAD_DIM ** -0.5)
    p = jax.nn.softmax(s, axis=-1).astype(v.dtype)
    return jnp.einsum('bhlm,bmhd->blhd', p, v).reshape(b, l, X_WIDTH)

def causal_depthwise_conv(x, w, bias):
    y = lax.conv_general_dilated(
        x, w[:, None, :].astype(x.dtype), window_strides=(1,),
        padding=[(SSM_CONV - 1, 0)], dimension_numbers=('NWC', 'WIO', 'NWC'),
        feature_group_count=x.shape[-1])
    return y + bias

def segsum_exp(a):
    l = a.shape[-1]
    cs = jnp.cumsum(a, axis=-1)
    mask = jnp.tril(jnp.ones((l, l), dtype=bool))
    return jnp.exp(jnp.where(mask, cs[..., :, None] - cs[..., None, :], -jnp.inf))

def ssd_chunked(x, dt, a, bm, cm):
    f32 = jnp.float32
    b, l = x.shape[0], x.shape[1]
    nc = l // CHUNK
    x = x.astype(f32).reshape(b, nc, CHUNK, SSM_GROUPS, SSM_HPG, SSM_HEAD_DIM)
    dt = dt.astype(f32).reshape(b, nc, CHUNK, SSM_GROUPS, SSM_HPG)
    bm = bm.astype(f32).reshape(b, nc, CHUNK, SSM_GROUPS, SSM_STATE)
    cm = cm.astype(f32).reshape(b, nc, CHUNK, SSM_GROUPS, SSM_STATE)
    xdt = x * dt[..., None]
    adt = jnp.moveaxis(dt * a.astype(f32).reshape(SSM_GROUPS, SSM_HPG), 2, -1)
    a_cs = jnp.cumsum(adt, axis=-1)
    cb = jnp.einsum('bclgn,bcsgn->bcgls', cm, bm)
    y_diag = jnp.einsum('bcgls,bcgrls,bcsgrp->bclgrp', cb, segsum_exp(adt), xdt)
    decay_to_end = jnp.exp(a_cs[..., -1:] - a_cs)
    decay_from_start = jnp.exp(a_cs)
    chunk_decay = jnp.exp(a_cs[..., -1])

    def step(h, inp):
        b_c, c_c, xdt_c, dte_c, dfs_c, cd_c = inp
        y_off = jnp.einsum('blgn,bgrpn,bgrl->blgrp', c_c, h, dfs_c)
        h = h * cd_c[..., None, None] + jnp.einsum('blgn,bgrl,blgrp->bgrpn', b_c, dte_c, xdt_c)
        return h, y_off

    h0 = jnp.zeros((b, SSM_GROUPS, SSM_HPG, SSM_HEAD_DIM, SSM_STATE), f32)
    xs = (jnp.moveaxis(bm, 1, 0), jnp.moveaxis(cm, 1, 0), jnp.moveaxis(xdt, 1, 0),
          jnp.moveaxis(decay_to_end, 1, 0), jnp.moveaxis(decay_from_start, 1, 0),
          jnp.moveaxis(chunk_decay, 1, 0))
    _, y_off = lax.scan(step, h0, xs)
    y = y_diag + jnp.moveaxis(y_off, 0, 1)
    return y.reshape(b, l, SSM_HEADS, SSM_HEAD_DIM)

def mamba2_mixer(proj, conv_w, conv_b, dt_bias, a_log, d_skip, gate_norm):
    b, l, _ = proj.shape
    z, xbc, dt = jnp.split(proj, [SSM_D_INNER, SSM_D_INNER + SSM_CONV_DIM], axis=-1)
    xbc = jax.nn.silu(causal_depthwise_conv(xbc, conv_w, conv_b))
    xs, bm, cm = jnp.split(xbc, [SSM_D_INNER, SSM_D_INNER + SSM_BC], axis=-1)
    dt = jax.nn.softplus(dt.astype(jnp.float32) + dt_bias.astype(jnp.float32))
    a = -jnp.exp(a_log.astype(jnp.float32))
    xh = xs.reshape(b, l, SSM_HEADS, SSM_HEAD_DIM)
    y = ssd_chunked(xh, dt, a, bm.reshape(b, l, SSM_GROUPS, SSM_STATE),
                    cm.reshape(b, l, SSM_GROUPS, SSM_STATE))
    y = (y + d_skip.astype(jnp.float32)[:, None] * xh.astype(jnp.float32)).astype(proj.dtype)
    yg = (y.reshape(b, l, SSM_D_INNER) * jax.nn.silu(z)).reshape(b, l, SSM_GROUPS, -1)
    return rmsnorm(yg, gate_norm.reshape(SSM_GROUPS, -1)).reshape(b, l, SSM_D_INNER)

def alibi_slopes(n_heads):
    return jnp.exp2(-8.0 * jnp.arange(1, n_heads + 1, dtype=jnp.float32) / n_heads)

def differential_attention(proj, q_norm, k_norm, lq1, lk1, lq2, lk2, sub_norm, lambda_init):
    f32 = jnp.float32
    b, l, _ = proj.shape
    q, k, v = jnp.split(proj, [DIFF_QK, 2 * DIFF_QK], axis=-1)
    q = rmsnorm(q.reshape(b, l, DIFF_HEADS, 2, DIFF_HEAD_DIM), q_norm)
    k = rmsnorm(k.reshape(b, l, DIFF_HEADS, 2, DIFF_HEAD_DIM), k_norm)
    v = v.reshape(b, l, DIFF_HEADS, DIFF_V_DIM)
    lam = (jnp.exp(jnp.sum(lq1.astype(f32) * lk1.astype(f32)))
           - jnp.exp(jnp.sum(lq2.astype(f32) * lk2.astype(f32))) + lambda_init)
    slopes = alibi_slopes(DIFF_HEADS)
    scale = DIFF_HEAD_DIM ** -0.5
    pos = jnp.arange(l)
    outs = []
    for qb in range(l // Q_BLOCK):
        q0, q1 = qb * Q_BLOCK, (qb + 1) * Q_BLOCK
        tq, tk = pos[q0:q1], pos[:q1]
        allowed = (tk[None, :] // CHUNK) <= (tq[:, None] // CHUNK)
        dist = jnp.abs(tq[:, None] - tk[None, :]).astype(f32)
        bias = jnp.where(allowed[None], -slopes[:, None, None] * dist[None], -jnp.inf)
        s = jnp.einsum('bqhmd,bkhmd->bhmqk', q[:, q0:q1], k[:, :q1]).astype(f32) * scale
        p = jax.nn.softmax(s + bias[:, None], axis=-1)
        attn = (p[:, :, 0] - lam * p[:, :, 1]).astype(v.dtype)
        outs.append(jnp.einsum('bhqk,bkhe->bqhe', attn, v[:, :q1]))
    o = rmsnorm(jnp.concatenate(outs, axis=1), sub_norm) * (1.0 - lambda_init)
    return o.reshape(b, l, DIFF_WIDTH)

def spatial_gating_mixer(proj, v_norm, w_s, b_s):
    b, l, _ = proj.shape
    u, v = jnp.split(jax.nn.gelu(proj, approximate=False), 2, axis=-1)
    v = rmsnorm(v.reshape(b, l, SGU_GROUPS, SGU_GROUP_DIM), v_norm.reshape(SGU_GROUPS, SGU_GROUP_DIM))
    v = v.reshape(b, l // SGU_BLOCK, SGU_BLOCK, SGU_GROUPS, SGU_GROUP_DIM)
    pos = jnp.arange(SGU_BLOCK)
    mask = (pos[None, :] // CHUNK) <= (pos[:, None] // CHUNK)
    ws = jnp.where(mask[None], w_s, 0.0).astype(v.dtype)
    mixed = jnp.einsum('gts,bnsgc->bntgc', ws, v) + b_s.T[:, :, None]
    return u * mixed.reshape(b, l, SGU_WIDTH)

def squared_relu_mlp(x, w1, w2):
    return jnp.square(jax.nn.relu(x @ w1)) @ w2

def setup_inputs(seed: int = 0) -> dict:
    key = jax.random.key(seed)
    ks = iter(jax.random.split(key, 48))
    f32 = jnp.float32

    def dense(shape, fan_in):
        return jax.random.normal(next(ks), shape, f32) * fan_in ** -0.5

    def gain(shape):
        return 1.0 + 0.02 * jax.random.normal(next(ks), shape, f32)

    def small(shape, s=0.02):
        return s * jax.random.normal(next(ks), shape, f32)

    dt0 = jnp.exp(jax.random.uniform(next(ks), (N_SSM, SSM_HEADS), f32,
                                     math.log(1e-3), math.log(1e-1)))
    return {
        'x': jax.random.normal(next(ks), (BATCH, SEQ, D_MODEL), f32),
        'mem': jax.random.normal(next(ks), (BATCH, MEM_LEN, D_MODEL), f32),
        'norm_mix': gain((DEPTH, D_MODEL)),
        'norm_ffn': gain((DEPTH, D_MODEL)),
        'mem_norm': gain((D_MODEL,)),
        'w_mem_kv': dense((DEPTH, D_MODEL, 2 * X_WIDTH), D_MODEL),
        'xq_norm': gain((DEPTH, X_HEAD_DIM)),
        'xk_norm': gain((DEPTH, X_HEAD_DIM)),
        'w_ff1': dense((DEPTH, D_MODEL, D_FF), D_MODEL),
        'w_ff2': dense((DEPTH, D_FF, D_MODEL), D_FF),
        'w_in_ssm': dense((N_SSM, D_MODEL, SSM_IN), D_MODEL),
        'ssm_conv_w': dense((N_SSM, SSM_CONV, SSM_CONV_DIM), SSM_CONV),
        'ssm_conv_b': small((N_SSM, SSM_CONV_DIM)),
        'ssm_dt_bias': dt0 + jnp.log(-jnp.expm1(-dt0)),
        'ssm_a_log': jnp.log(jax.random.uniform(next(ks), (N_SSM, SSM_HEADS), f32, 1.0, 16.0)),
        'ssm_d': gain((N_SSM, SSM_HEADS)),
        'ssm_gate_norm': gain((N_SSM, SSM_D_INNER)),
        'w_out_ssm': dense((N_SSM, SSM_D_INNER + X_WIDTH, D_MODEL), SSM_D_INNER + X_WIDTH),
        'w_in_diff': dense((N_DIFF, D_MODEL, DIFF_IN), D_MODEL),
        'diff_q_norm': gain((N_DIFF, DIFF_HEAD_DIM)),
        'diff_k_norm': gain((N_DIFF, DIFF_HEAD_DIM)),
        'diff_lq1': small((N_DIFF, DIFF_HEAD_DIM), 0.1),
        'diff_lk1': small((N_DIFF, DIFF_HEAD_DIM), 0.1),
        'diff_lq2': small((N_DIFF, DIFF_HEAD_DIM), 0.1),
        'diff_lk2': small((N_DIFF, DIFF_HEAD_DIM), 0.1),
        'diff_sub_norm': gain((N_DIFF, DIFF_V_DIM)),
        'w_out_diff': dense((N_DIFF, DIFF_WIDTH + X_WIDTH, D_MODEL), DIFF_WIDTH + X_WIDTH),
        'w_in_sgu': dense((N_SGU, D_MODEL, SGU_IN), D_MODEL),
        'sgu_v_norm': gain((N_SGU, SGU_WIDTH)),
        'sgu_w_s': dense((N_SGU, SGU_GROUPS, SGU_BLOCK, SGU_BLOCK), SGU_BLOCK),
        'sgu_b_s': gain((N_SGU, SGU_GROUPS, SGU_BLOCK)),
        'w_out_sgu': dense((N_SGU, SGU_WIDTH + X_WIDTH, D_MODEL), SGU_WIDTH + X_WIDTH),
    }

def reference(x, mem, norm_mix, norm_ffn, mem_norm, w_mem_kv, xq_norm, xk_norm, w_ff1, w_ff2,
              w_in_ssm, ssm_conv_w, ssm_conv_b, ssm_dt_bias, ssm_a_log, ssm_d, ssm_gate_norm, w_out_ssm,
              w_in_diff, diff_q_norm, diff_k_norm, diff_lq1, diff_lk1, diff_lq2, diff_lk2, diff_sub_norm,
              w_out_diff, w_in_sgu, sgu_v_norm, sgu_w_s, sgu_b_s, w_out_sgu):
    mem_n = rmsnorm(mem, mem_norm)
    for i in range(DEPTH):
        kind, j = i % N_MIXERS, i // N_MIXERS
        h = rmsnorm(x, norm_mix[i])
        if kind == 0:
            proj = h @ w_in_ssm[j]
            mix_in, xq = proj[..., :-X_WIDTH], proj[..., -X_WIDTH:]
            mix_out = mamba2_mixer(mix_in, ssm_conv_w[j], ssm_conv_b[j], ssm_dt_bias[j],
                                   ssm_a_log[j], ssm_d[j], ssm_gate_norm[j])
            w_out = w_out_ssm[j]
        elif kind == 1:
            proj = h @ w_in_diff[j]
            mix_in, xq = proj[..., :-X_WIDTH], proj[..., -X_WIDTH:]
            lambda_init = 0.8 - 0.6 * math.exp(-0.3 * i)
            mix_out = differential_attention(mix_in, diff_q_norm[j], diff_k_norm[j], diff_lq1[j],
                                             diff_lk1[j], diff_lq2[j], diff_lk2[j],
                                             diff_sub_norm[j], lambda_init)
            w_out = w_out_diff[j]
        else:
            proj = h @ w_in_sgu[j]
            mix_in, xq = proj[..., :-X_WIDTH], proj[..., -X_WIDTH:]
            mix_out = spatial_gating_mixer(mix_in, sgu_v_norm[j], sgu_w_s[j], sgu_b_s[j])
            w_out = w_out_sgu[j]
        cross = memory_cross_attention(xq, mem_n, w_mem_kv[i], xq_norm[i], xk_norm[i])
        x = x + jnp.concatenate([mix_out, cross], axis=-1) @ w_out
        x = x + squared_relu_mlp(rmsnorm(x, norm_ffn[i]), w_ff1[i], w_ff2[i])
    return x


_drawn_inputs = setup_inputs


def setup_inputs(seed=0):
    import zlib

    import numpy as np

    out = dict(_drawn_inputs(seed))
    spreads = {}
    factors = {'mem_norm': 8.0,
     'xq_norm': 8.0,
     'xk_norm': 8.0,
     'ssm_d': 6.577,
     'ssm_gate_norm': 3.225,
     'diff_q_norm': 8.0,
     'diff_k_norm': 8.0,
     'diff_lq1': 7.346,
     'diff_lk1': 8.0,
     'diff_sub_norm': 8.0,
     'sgu_v_norm': 28.512,
     'sgu_b_s': 25.061}
    for name, (base, spread) in spreads.items():
        noise = np.random.default_rng([zlib.crc32(name.encode()), seed]).standard_normal(out[name].shape)
        drawn = base * np.exp(spread * noise) if base else spread * noise
        out[name] = __import__('jax').numpy.asarray(drawn.astype(out[name].dtype))
    for name, factor in factors.items():
        out[name] = (out[name] * factor).astype(out[name].dtype)
    return out
```

```python
import math
from contextlib import ExitStack

import numpy as np

import concourse.bass as bass
from concourse import mybir

F32 = mybir.dt.float32
F32R = mybir.dt.float32r
I32 = mybir.dt.int32
ALU = mybir.AluOpType
ACT = mybir.ActivationFunctionType
AX = mybir.AxisListType

P = 128
D, SEQ, DEPTH, DFF = 1024, 256, 4, 4096
MEM = 256
TT = SEQ // P
XH, XD = 4, 256
DIN, SH, SG, SHD, SN, TAPS = 2048, 32, 8, 64, 128, 4
HPG = SH // SG
GW = DIN // SG
BC = SG * SN
XBC = DIN + 2 * BC
DH, DHD = 8, 64
SGG, SGW = 8, 128
EPS = 1e-6
COLS = 512
UK = 2
UNIT = UK * COLS
RING = 4
KIND = [i % 3 for i in range(DEPTH)]
SSM, DIFF, SGU = 0, 1, 2
MIXT = {SSM: DIN // P, DIFF: D // P, SGU: D // P}
CROSS0 = 16
LAMBDA_INIT = 0.8 - 0.6 * math.exp(-0.3 * 1)
RSQRT_SEED = float(0x5F3759DF)

PC = {}
_n = 0
for _name, _w in (("norm_mix", DEPTH * 8), ("norm_ffn", DEPTH * 8), ("mem_norm", 8), ("xq", DEPTH * 2), ("xk", DEPTH * 2),
                  ("conv_w", 2 * TAPS * 32), ("conv_b", 2 * 32), ("gate", 2 * 16), ("dq", 1), ("dk", 1), ("dsub", 1), ("b_s", 8)):
    PC[_name] = _n
    _n += _w
NPC = _n
RW = {"dt_bias": 0, "a_log": 64, "ssm_d": 128, "lq1": 192, "lk1": 256, "lq2": 320, "lk2": 384}
NRW = 448
CN = {"ident": 0, "upto": 128, "after": 256, "dist": 384, "sgu_mask": 384 + 384}
NCN = CN["sgu_mask"] + 128


class Job:

    def __init__(self, plan, banks, act, dve, read_now=True):
        plan.n_jobs += 1
        self.banks, self.done, self.act, self.dve = banks, plan.n_jobs, 0, 0
        self.readers = (act, dve)
        if read_now:
            self.read(plan)
        self.before = []
        for b in banks:
            if b in plan.last and plan.last[b] not in self.before:
                self.before.append(plan.last[b])
            plan.last[b] = self

    def read(self, plan):
        act, dve = self.readers
        if act:
            plan.n_act += 1
            self.act = plan.n_act
        if dve:
            plan.n_dve += 1
            self.dve = plan.n_dve


class Plan:

    def __init__(self):
        self.steps, self.units, self.release = [], [], []
        self.n_jobs = self.n_act = self.n_dve = self.n_used = 0
        self.last, self.pair, self.fpair, self.misc = {}, 0, 1, 0
        self.nt_free = 0
        self.n = {}
        self.build()

    def count(self, what):
        self.n[what] = self.n.get(what, 0) + 1
        return self.n[what]

    def step(self, kind, **kw):
        kw["kind"] = kind
        kw["w"] = len(self.units)
        self.steps.append(kw)
        return kw

    def stream_job(self, act, dve, read_now=True):
        self.pair ^= 1
        return Job(self, (2 * self.pair, 2 * self.pair + 1), act, dve, read_now)

    def misc_job(self, act, dve):
        self.misc = (self.misc + 1) % 4
        return Job(self, (4 + self.misc,), act, dve)

    def take(self, units, job, last=True):
        first = len(self.units)
        for n, u in enumerate(units):
            self.units.append(u)
            if last and n == len(units) - 1:
                self.release.append(("job", job.done))
            else:
                self.n_used += 1
                self.release.append(("used", self.n_used))
        return list(range(first, len(self.units)))

    def add(self, ev):
        if ev:
            if ev["kind"] == "evac":
                ev["job"].read(self)
            ev["w"] = len(self.units)
            self.steps.append(ev)

    def gemm(self, form, src, weight, col, evac, act, dve, **kw):
        job = self.stream_job(act, dve, read_now=False)
        us = self.take([(weight, k * UK, col) for k in range(D // P // UK)], job)
        self.step("gemm", form=form, src=src, job=job, us=us)
        return dict(kind="evac", job=job, evac=evac, **kw)

    def block(self, form, src, weight, col, evac, late=None, **kw):
        ev = self.gemm(form, src, weight, col, evac, True, False, **kw)
        self.add(ev)
        self.turn(late)
        return ev

    def normed(self, src, weight, col, groups, dst, tile, gain, late=None):
        ev = self.gemm("nat", src, weight, col, "norm", True, True, groups=groups)
        self.turn(late)
        self.add(ev)
        return dict(kind="turn", nt=ev["job"].dve, dst=dst, tile=tile, gain=gain)

    def turn(self, t):
        if t:
            t["jobs"] = [self.misc_job(True, False) for _ in range(2)]
            self.nt_free = t["jobs"][-1].act
            self.add(t)

    def kv(self, i, n, late=None):
        wk = ("w_mem_kv", i)
        if n < 2:
            return self.normed("mem", wk, n * COLS, 2, "kT", 4 * n, ("xk", i), late)
        self.block("nat", "mem", wk, n * COLS, "v", late, nb=n - 2)
        return None

    def split_turn(self, src, ready, ntiles, dst, gain):
        self.step("split_turn", src=src, ready=ready, dst=dst, gain=gain, jobs=[self.misc_job(True, True) for _ in range(ntiles // 2)])

    def norm(self, what, x_dve=0):
        n = self.count("norm")
        self.step("norm", what=what, n=n, x_dve=x_dve)
        return ("xn_new", n)

    def cross(self, i):
        kv_q = self.n_act
        pT = {}
        for k in range(XH + 2):
            if k < XH:
                self.step("x_score", n=i * XH + k, h=k, kv_q=kv_q, job=self.misc_job(True, True))
            if 0 <= k - 1 < XH:
                pT[k - 1] = self.misc_job(True, False)
                self.step("x_turn", n=i * XH + k - 1, job=pT[k - 1])
            if 0 <= k - 2:
                self.step("x_out", n=i * XH + k - 2, h=k - 2, pT=pT[k - 2].act, job=self.misc_job(True, True))

    def build(self):
        ready = self.norm("mem")
        self.split_turn("xn", ready, 8, "memT", ("mem_norm", 0))
        late = self.kv(0, 0)
        count = {SSM: 0, DIFF: 0, SGU: 0}
        x_dve = 0
        for i in range(DEPTH):
            kind, l = KIND[i], count[KIND[i]]
            count[kind] += 1
            self.step("layer", i=i, mixer=kind, l=l, n=i + 1, ff=self.n.get("ff", 0))
            ready = self.norm("x", x_dve)
            late = self.kv(i, 1, late)
            self.split_turn("xn", ready, 8, "hT", ("norm_mix", 8 * i))
            (self.ssm, self.diff, self.sgu)[kind](i, l, late)
            x_dve = self.out_projection(i, l, kind)
            ready = self.norm("x", x_dve)
            late = self.kv(i + 1, 0) if i + 1 < DEPTH else None
            self.split_turn("xn", ready, 8, "hT", ("norm_ffn", 8 * i))
            self.turn(late)
            late = None
            x_dve = self.ffn(i)
        self.x_dve = x_dve

    def query(self, i, weight, col, n, late=None):
        return self.normed("hT", weight, col + n * COLS, 2, "qT", 4 * n, ("xq", i), late)

    def ssm(self, i, l, late):
        w = ("w_in_ssm", l)
        job = self.stream_job(False, True)
        us = self.take([("dt", l, 0)], job)
        self.step("gemm", form="dt", src="hT", job=job, us=us)
        self.step("evac", job=job, evac="dt")
        self.turn(late)
        self.step("dt_turn", l=l, i=i, n=l + 1, dtT=job.dve, nt_free=self.nt_free, job=self.misc_job(False, True))

        def conv(ft):
            ev = self.gemm("feat", "hT", w, DIN + ft * P, "conv", True, True, l=l, ft=ft)
            return ev, dict(kind="silu", ft=ft, job=ev["job"])
        silu = None
        for k in range(4):
            self.block("nat", "hT", w, k * COLS, "z", nb=k)
            self.add(silu)
            if k == 0:
                self.step("decay", l=l, n=l + 1, job=self.misc_job(True, False))
            taps, silu = conv(16 + 4 * k)
            self.add(taps)

        def xs_turn(k):
            jobs = [self.misc_job(True, False) for _ in range(TT)]
            self.step("xs_turn", k=k, conv=l * 8 + 5 + k, jobs=jobs)
            return jobs[-1].act
        xs_act = {}

        def ssd_a(g):
            jobs = {}
            for b in range(TT):
                jobs["S", b] = self.misc_job(True, False)
                jobs["C", b] = self.misc_job(False, True)
            jobs["B"] = self.misc_job(True, False)
            self.step("ssd_a", g=g, l=l, n=l * SG + g, xs=xs_act[g // 2], jobs=jobs)
            self.bn = jobs["B"].act

        def ssd_b(g):
            jobs = {q: self.misc_job(q == "H", q != "H") for q in ("H", ("Y", 0), ("Y", 1), "O")}
            self.step("ssd_b", g=g, n=l * SG + g, bn=self.bn, jobs=jobs)

        def group(g):
            if g >= 1:
                ssd_b(g - 1)
            ssd_a(g)
            if g >= 1:
                self.step("yg_square", g=g - 1, n=l * SG + g - 1)
        late, taps = None, None
        for s, (what, k) in enumerate([("xs", k) for k in range(4)] + [("q", 0), ("q", 1), ("kv", 2), ("kv", 3)]):
            g = s - 1
            if g >= 0:
                self.step("ssd_mv", g=g)
            if what == "xs":
                taps, new = conv(4 * k)
            elif what == "q":
                late = self.query(i, w, DIN + XBC + SH, k, late)
            else:
                late = self.kv(i, k, late)
            if silu:
                self.add(silu)
                if silu["ft"] < 16:
                    xs_act[silu["ft"] // 4] = xs_turn(silu["ft"] // 4)
                silu = None
            if what == "xs":
                self.add(taps)
                silu = new
            if g >= 0:
                group(g)
        self.step("ssd_mv", g=7)
        group(7)
        ssd_b(7)
        self.step("yg_square", g=7, n=l * SG + 7)
        n = self.count("gn")
        self.step("group_norm", what=SSM, l=l)
        self.cross(i)
        self.split_turn("mix", ("mix_new", n), 16, "act", ("gate", 16 * l))

    def diff(self, i, l, late):
        w = ("w_in_diff", l)
        heads, prev, qk = iter(range(DH)), [None], {}

        def head():
            h = next(heads, None)
            if prev[0] is not None:
                jobs = [self.misc_job(True, False) for _ in range(2)]
                self.step("d_out", h=prev[0], jobs=jobs)
                self.o_act = jobs[1].act
            if h is not None:
                self.step("d_score", h=h, qk=qk[h // 4], jobs=[self.misc_job(False, True) for _ in range(2)])
            prev[0] = h
        for half in range(2):
            late = self.normed("hT", w, half * COLS, 8, "dq", 4 * half, ("dq", 0), late)
            if half:
                head()
            late = self.normed("hT", w, D + half * COLS, 8, "dk", 4 * half, ("dk", 0), late)
            if half:
                head()
            late = self.block("nat", "hT", w, 2 * D + half * COLS, "dv", late, nb=half) and None
            qk[half] = self.n_act
            if half:
                head()
        for n in range(2):
            late = self.query(i, w, 3 * D, n, late)
            head()
        for n in (2, 3):
            late = self.kv(i, n, late)
            head()
        head()
        head()
        n = self.count("gn")
        self.step("group_norm", what=DIFF, o_act=self.o_act)
        self.cross(i)
        self.split_turn("mix", ("mix_new", n), 8, "act", ("dsub", 0))

    def sgu(self, i, l, late):
        w = ("w_in_sgu", l)
        for n in (2, 3, 0, 1):
            ev = self.block("nat", "hT", w, n * COLS, "gelu", late, nb=n)
            late = None
            if n == 3:
                self.step("sgu_norm", v_act=ev["job"].act)
        late = self.query(i, w, 2 * D, 0)
        jobs = [self.misc_job(False, True) for _ in range(4)]
        self.step("sgu_mix", u_act=ev["job"].act, jobs=jobs)
        late = self.query(i, w, 2 * D, 1, late)
        late = self.kv(i, 2, late)
        self.kv(i, 3)
        self.cross(i)
        self.split_turn("mix", ("dve_free", jobs[-1].dve), 8, "act", None)

    def out_projection(self, i, l, kind):
        name = ("w_out_ssm", "w_out_diff", "w_out_sgu")[kind]
        nt = MIXT[kind]
        tiles = [(nt + k, CROSS0 + k) for k in range(0, 8, UK)] + [(k, k) for k in range(0, nt, UK)]
        job = Job(self, (0, 1, 2, 3), False, True)
        self.pair = 1
        us = self.take([((name, l), wt, nb * COLS) for wt, _ in tiles for nb in range(2)], job)
        self.step("out", job=job, us=us, src=[at for _, at in tiles for _ in range(2)])
        return job.dve

    def ffn(self, i):
        nblk = DFF // COLS
        acc = Job(self, (0, 1, 2, 3), False, True)
        self.n_jobs -= 1
        base = self.n.get("ff", 0)

        def up(b):
            self.fpair ^= 1
            job = Job(self, (4 + 2 * self.fpair, 5 + 2 * self.fpair), True, False)
            us = self.take([(("w_ff1", i), k * UK, b * COLS) for k in range(D // P // UK)], job)
            self.step("gemm", form="feat", src="hT", job=job, us=us)
            self.step("evac", evac="relu2", job=job, nf=self.count("ff"), b=b)

        def down(b):
            last = b == nblk - 1
            if last:
                self.n_jobs += 1
                acc.done = self.n_jobs
            us = self.take([(("w_ff2", i), 4 * b + k, nb * COLS) for k in (0, 2) for nb in range(2)], acc, last)
            self.step("down", job=acc, us=us, b=b, nf=base + b + 1, first=b == 0, last=last)
        for b in range(4):
            up(b)
        for b in range(4, nblk):
            down(b - 4)
            up(b)
        for b in range(4, nblk):
            down(b)
        self.pair, self.misc = 1, 3
        return acc.dve


def bass_trunk(nc, A, out):
    plan = Plan()
    steps, NU = plan.steps, len(plan.units)
    ctx = ExitStack()
    with ctx:
        at = [-(-nc.sbuf_base // 64) * 64]

        def sb(name, shape, dt=F32, offset=None):
            size = -(-int(np.prod(shape[1:])) * 4 // 32) * 32
            if offset is None:
                offset = at[0]
                at[0] += size
            return nc.alloc_sbuf_tensor_at(name, shape, dt, offset=offset)

        def here():
            return at[0]

        x = sb("x", [P, TT, D])
        o_hT = here()
        hT = (sb("hT_hi", [P, 8, SEQ], F32R), sb("hT_lo", [P, 8, SEQ], F32R))
        o_act = here()
        act_hi = sb("act_hi", [P, 24, SEQ], F32R)
        act_lo = sb("act_lo", [P, 24, SEQ], F32R)
        actT = (act_hi, act_lo)
        memT = (sb("memT_hi", [P, 8, MEM], F32R), sb("memT_lo", [P, 8, MEM], F32R))
        kT = sb("kT", [P, 8, MEM])
        v = sb("v", [P, TT, D])
        raw = sb("raw", [P, RING, UNIT])
        w_hi_t = sb("w_hi_t", [P, RING, UNIT], F32R)
        w_lo_t = sb("w_lo_t", [P, RING, UNIT], F32R)
        mix = sb("mix", [P, TT, DIN])
        qT = sb("qT", [P, 8, SEQ])
        consts = sb("consts_sb", [P, NCN])
        pc = sb("percol_sb", [P, NPC])
        rw = sb("rows_sb", [P, NRW])
        st = sb("stats", [P, 320])
        nt = sb("nt", [P, TT, COLS])
        o_s1 = here()
        at[0] += 4096
        o_s2 = here()
        at[0] += 8192
        xdt = sb("xdt", [P, TT, GW])
        xw = sb("xw", [P, GW])
        Bn = sb("Bn", [P, P])
        hst = sb("hst", [P, GW])
        cbm = sb("cbm", [P, TT, P])
        junk = sb("junk", [P, GW])
        assert here() <= nc.sbuf_usable_end, here() - nc.sbuf_usable_end
        bcT = sb("bcT", [P, 16, SEQ], F32, o_act)
        xs = sb("xs", [P, TT, DIN], F32, o_act + 24 * SEQ * 4)
        dqT = sb("dqT", [P, 8, SEQ], F32, o_act)
        dkT = sb("dkT", [P, 8, SEQ], F32, o_act + 8 * SEQ * 4)
        dv = sb("dv", [P, TT, D], F32, o_act + 24 * SEQ * 4)
        xp = sb("xp", [P, 2, 2 * SEQ], F32, o_hT)
        xpT = sb("xpT", [P, 2, 2 * SEQ], F32, o_hT + 4096)
        xsT = sb("xsT", [P, 4, SEQ], F32, o_s1)
        mv = sb("mv", [P, TT, HPG * P], F32, o_s2)
        E = sb("E", [P, TT, HPG * P], F32, o_s2 + 4096)
        dS = sb("dS", [P, 2, 2, 384], F32, o_s2)
        daT = sb("daT", [P, 384], F32, o_s2 + 6144)
        rf = [sb("rf0", [P, 4 * SEQ], F32, o_s1), sb("rf1", [P, 4 * SEQ], F32, o_s2)]
        wsT = sb("wsT", [P, SGG, P], F32, o_s1)
        sgain = sb("sgain", [P, D], F32, o_s2)

        cur = [0]

        def stat(n):
            cur[0] += n
            assert cur[0] <= 320
            return st[:, cur[0] - n:cur[0]]

        ss, r_x = stat(2), stat(2)
        ta, tb = stat(16), stat(16)
        ssn, r_nt = stat(16), stat(16)
        xmx, xnb, xsum, xrs = stat(2), stat(4), stat(4), stat(2)
        dnb, dsm, drs = stat(8), stat(8), stat(4)
        ssy, r_y = stat(16), stat(16)
        gq8, gx16, gsub, lam, lam2 = stat(1), stat(8), stat(1), stat(2), stat(1)
        expa, decay = stat(32), stat(64)
        dts = [nt[:, 0, 64 * k:64 * k + 64] for k in range(8)]
        dt_keep = sb("dt_keep", [P, 128])
        dt_v, adt = dt_keep[:, 0:64], dt_keep[:, 64:128]
        dtT = sb("dtT", [P, SEQ], F32, o_s1)
        assert here() <= nc.sbuf_usable_end, here() - nc.sbuf_usable_end

        ps = ctx.enter_context(nc.psum_tensor("ps", [P, 8, 512], F32))

        def sem(name):
            return ctx.enter_context(nc.semaphore(name))

        raw_in = [sem(f"raw_in{s}") for s in range(RING)]
        w_hi, w_lo, w_used = sem("w_hi"), sem("w_lo"), sem("w_used")
        job_done, act_free, dve_free = sem("job_done"), sem("act_free"), sem("dve_free")
        loaded, loaded2, stored = sem("loaded"), sem("loaded2"), sem("stored")
        act_chain, dve_chain = sem("act_chain"), sem("dve_chain")
        setup_done, expa_done = sem("setup_done"), sem("expa_done")
        sumsq, xn_new = sem("sumsq"), sem("xn_new")
        conv_out = sem("conv_out")
        dt_abs, dt_exp, adt_new = sem("dt_abs"), sem("dt_exp"), sem("adt_new")
        mv_new, m_new, xdt_new, yg_new, yg_sq = sem("mv_new"), sem("m_new"), sem("xdt_new"), sem("yg_new"), sem("yg_sq")
        mix_new, x_pn = sem("mix_new"), sem("x_pn")
        d_nb, d_p, d_a = sem("d_nb"), sem("d_p"), sem("d_a")
        ff_r, ff_f, ff_hi, ff_lo = sem("ff_r"), sem("ff_f"), sem("ff_hi"), sem("ff_lo")
        sg_in, sg_w, sg_v = sem("sg_in"), sem("sg_w"), sem("sg_v")
        ready_sems = {"xn_new": xn_new, "mix_new": mix_new, "dve_free": dve_free}

        ident = consts[:, CN["ident"]:CN["ident"] + P]
        upto = consts[:, CN["upto"]:CN["upto"] + P]
        after = consts[:, CN["after"]:CN["after"] + P]
        dist = consts[:, CN["dist"]:CN["dist"] + 384]
        sgu_mask = consts[:, CN["sgu_mask"]:CN["sgu_mask"] + P]

        def col(name, k=0):
            return pc[:, PC[name] + k:PC[name] + k + 1]

        def src_view(name):
            return {"xn": mix[:, :, 0:D], "mix": mix[:, :, :]}[name]

        T = {"memT": memT, "hT": hT, "act": actT}

        def gains(step, pair):
            g = step["gain"]
            if g is None:
                return None
            if g[0] == "dsub":
                return [gsub, gsub]
            return [col(g[0], g[1] + 2 * pair), col(g[0], g[1] + 2 * pair + 1)]

        def turn_gains(step, pair):
            name, i = step["gain"]
            if name == "dq":
                return [gq8, gq8]
            if name == "dk":
                return [col("dk"), col("dk")]
            if name == "xq":
                return [gx16[:, 2 * i:2 * i + 1], gx16[:, 2 * i + 1:2 * i + 2]]
            return [col("xk", 2 * i), col("xk", 2 * i + 1)]

        block = ctx.enter_context(nc.Block())

        @block.sync
        def _(sp):
            sp.dma_start(mix[:, :, D:2 * D], A["mem"].rearrange("a (t p) d -> p (a t) d", p=P)).then_inc(loaded, 16)
            sp.dma_start(consts[:, :], A["consts"]).then_inc(loaded, 16)
            sp.dma_start(pc[:, :], A["percol"]).then_inc(loaded, 16)
            sp.dma_start(rw[:, :], A["rows"].partition_broadcast(P)).then_inc(loaded, 16)
            for u in range(RING):
                sp.dma_start(raw[:, u, :], A["wstream"][u]).then_inc(raw_in[u], 16)
            sp.dma_start(x[:, :, :], A["x"].rearrange("a (t p) d -> p (a t) d", p=P)).then_inc(loaded2, 16)
            with sp.Fori(1, NU // RING) as it:
                for s in range(RING):
                    sp.wait_ge(w_lo, it * RING + (s - RING + 1))
                    sp.dma_start(raw[:, s, :], A["wstream"][bass.ds(it * RING + s, 1)].rearrange("a p n -> p (a n)"))\
                        .then_inc(raw_in[s], 16)
            for u in range(NU // RING * RING, NU):
                sp.wait_ge(w_lo, u - RING + 1)
                sp.dma_start(raw[:, u % RING, :], A["wstream"][u]).then_inc(raw_in[u % RING], 16)
            for t in range(TT):
                sp.wait_ge(dve_free, plan.x_dve)
                sp.dma_start(out.rearrange("a (t p) d -> p (a t) d", p=P)[:, t], x[:, t, :]).then_inc(stored, 16)
            sp.wait_ge(stored, 16 * TT)

        @block.gpsimd
        def _(pool):
            def lo(slot):
                return pool.tensor_tensor(w_lo_t[:, slot, :], raw[:, slot, :], w_hi_t[:, slot, :].bitcast(F32), ALU.subtract)
            with pool.Fori(0, NU // RING) as it:
                for s in range(RING):
                    pool.wait_ge(w_hi, it * RING + (s + 1))
                    lo(s).then_inc(w_lo, 1)
            for u in range(NU // RING * RING, NU):
                pool.wait_ge(w_hi, u + 1)
                lo(u % RING).then_inc(w_lo, 1)

        @block.tensor
        def _(pe):
            def banks_free(job):
                for b in job.before:
                    if b.act:
                        pe.wait_ge(act_free, b.act)
                    if b.dve:
                        pe.wait_ge(dve_free, b.dve)

            def unit(u):
                pe.wait_ge(w_hi, u + 1)
                pe.wait_ge(w_lo, u + 1)
                s = u % RING
                return (w_hi_t[:, s, :].rearrange("p (k n) -> p k n", k=UK), w_lo_t[:, s, :].rearrange("p (k n) -> p k n", k=UK))

            def release(u, mm):
                kind, _ = plan.release[u]
                mm.then_inc(w_used if kind == "used" else job_done, 1)

            def natural(bank_of, act, k0, us, first, last):
                for n, u in enumerate(us):
                    wh, wl = unit(u)
                    for k in range(UK):
                        for t in range(TT):
                            a = [part[:, k0[n] + k, t * P:(t + 1) * P] for part in act]
                            begin = first(n) and k == 0
                            end = last(n) and k == UK - 1
                            pe.matmul(ps[:, bank_of(n, t), :], a[0], wh[:, k, :], start=begin, stop=False)
                            pe.matmul(ps[:, bank_of(n, t), :], a[0], wl[:, k, :], start=False, stop=False)
                            mm = pe.matmul(ps[:, bank_of(n, t), :], a[1], wh[:, k, :], start=False, stop=end)
                    release(u, mm)

            def featured(job, act, us):
                for n, u in enumerate(us):
                    wh, wl = unit(u)
                    for k in range(UK):
                        kt = UK * n + k
                        for f in range(4):
                            o = ps[:, job.banks[f // 2], (f % 2) * SEQ:(f % 2 + 1) * SEQ]
                            c = slice(f * P, (f + 1) * P)
                            pe.matmul(o, wh[:, k, c], act[0][:, kt, :], start=kt == 0 and f % 2 == 0, stop=False, skip_group_check=True)
                            pe.matmul(o, wh[:, k, c], act[1][:, kt, :], start=False, stop=False, skip_group_check=True)
                            mm = pe.matmul(o, wl[:, k, c], act[0][:, kt, :], start=False, stop=kt == 7, skip_group_check=True)
                    release(u, mm)

            split_jobs = {}
            pe.wait_ge(loaded, 64)
            for s in steps:
                k = s["kind"]
                if k == "gemm":
                    banks_free(s["job"])
                    act = T[{"mem": "memT", "hT": "hT"}[s["src"]]]
                    j = split_jobs[s["src"]]
                    pe.wait_ge(act_free, j.act)
                    pe.wait_ge(dve_free, j.dve)
                    if s["form"] == "nat":
                        b = s["job"].banks
                        natural(lambda n, t: b[t], act, [UK * n for n in range(4)], s["us"], lambda n: n == 0, lambda n: n == 3)
                    elif s["form"] == "feat":
                        featured(s["job"], act, s["us"])
                    else:
                        wh, wl = unit(s["us"][0])
                        wh, wl = (w.rearrange("p k n -> p (k n)").rearrange("p (k n) -> p k n", k=8) for w in (wh, wl))
                        o = ps[:, s["job"].banks[0], 0:SEQ]
                        for kt in range(8):
                            pe.matmul(o, wh[:, kt, :], act[0][:, kt, :], start=kt == 0, stop=False)
                            pe.matmul(o, wh[:, kt, :], act[1][:, kt, :], start=False, stop=False)
                            mm = pe.matmul(o, wl[:, kt, :], act[0][:, kt, :], start=False, stop=kt == 7)
                        release(s["us"][0], mm)
                elif k == "split_turn":
                    pe.wait_ge(ready_sems[s["ready"][0]], s["ready"][1])
                    src = src_view(s["src"])
                    for m, job in enumerate(s["jobs"]):
                        banks_free(job)
                        for f in range(2):
                            for t in range(TT):
                                mm = pe.transpose(ps[:, job.banks[0], f * SEQ + t * P:f * SEQ + (t + 1) * P],
                                                  src[:, t, (2 * m + f) * P:(2 * m + f + 1) * P], ident)
                        mm.then_inc(job_done, 1)
                    split_jobs[{"memT": "mem", "hT": "hT", "act": "act"}[s["dst"]]] = s["jobs"][-1]
                elif k == "turn":
                    pe.wait_ge(dve_free, s["nt"])
                    for m, job in enumerate(s["jobs"]):
                        banks_free(job)
                        for f in range(2):
                            for t in range(TT):
                                mm = pe.transpose(ps[:, job.banks[0], f * SEQ + t * P:f * SEQ + (t + 1) * P],
                                                  nt[:, t, (2 * m + f) * P:(2 * m + f + 1) * P], ident)
                        mm.then_inc(job_done, 1)
                elif k == "dt_turn":
                    banks_free(s["job"])
                    pe.wait_ge(dve_free, s["dtT"])
                    for t in range(TT):
                        mm = pe.transpose(ps[:, s["job"].banks[0], t * SH:(t + 1) * SH], dtT[0:SH, t * P:(t + 1) * P], ident[0:SH, 0:SH])
                    mm.then_inc(job_done, 1)
                elif k == "decay":
                    banks_free(s["job"])
                    pe.wait_ge(adt_new, s["n"])
                    b = s["job"].banks[0]
                    pe.matmul(ps[:, b, 0:SH], after, adt[:, 0:SH], start=True, stop=True)
                    pe.matmul(ps[:, b, SH:2 * SH], upto, adt[:, SH:2 * SH], start=True, stop=True).then_inc(job_done, 1)
                elif k == "xs_turn":
                    pe.wait_ge(conv_out, s["conv"])
                    for t, job in enumerate(s["jobs"]):
                        banks_free(job)
                        for f in range(4):
                            mm = pe.transpose(ps[:, job.banks[0], f * P:(f + 1) * P], xsT[:, f, t * P:(t + 1) * P], ident)
                        mm.then_inc(job_done, 1)
                elif k == "ssd_a":
                    g, n = s["g"], s["n"]
                    for b in range(TT):
                        job = s["jobs"]["S", b]
                        banks_free(job)
                        pe.wait_ge(mv_new, n + 1)
                        pe.matmul(ps[:, job.banks[0], :], after, mv[:, b, :], start=True, stop=True).then_inc(job_done, 1)
                        job = s["jobs"]["C", b]
                        banks_free(job)
                        pe.wait_ge(conv_out, s["l"] * 8 + 4)
                        tok = slice(b * P, (b + 1) * P)
                        pe.matmul(ps[:, job.banks[0], 0:P], bcT[:, g, tok], bcT[:, 8 + g, tok], start=True, stop=True).then_inc(job_done, 1)
                    job = s["jobs"]["B"]
                    banks_free(job)
                    pe.transpose(ps[:, job.banks[0], 0:P], bcT[:, g, 0:P], ident).then_inc(job_done, 1)
                elif k == "ssd_b":
                    g, n, jobs = s["g"], s["n"], s["jobs"]
                    banks_free(jobs["H"])
                    pe.wait_ge(xdt_new, n + 1)
                    pe.wait_ge(act_free, s["bn"])
                    pe.matmul(ps[:, jobs["H"].banks[0], 0:GW], Bn[:, :], xw[:, :], start=True, stop=True).then_inc(job_done, 1)
                    for b in range(TT):
                        job = jobs["Y", b]
                        banks_free(job)
                        pe.wait_ge(m_new, 2 * n + b + 1)
                        for h in range(HPG):
                            c0 = h * P - (h % 2) * SHD
                            mm = pe.matmul(ps[:, job.banks[0], c0:c0 + P], E[:, b, h * P:(h + 1) * P],
                                           xdt[:, b, (h // 2) * P:(h // 2 + 1) * P], start=True, stop=True, skip_group_check=True)
                        mm.then_inc(job_done, 1)
                    job = jobs["O"]
                    banks_free(job)
                    pe.wait_ge(act_free, jobs["H"].act)
                    pe.matmul(ps[:, job.banks[0], 0:GW], bcT[:, 8 + g, P:2 * P], hst[:, :], start=True, stop=True).then_inc(job_done, 1)
                elif k == "d_score":
                    h = s["h"]
                    pe.wait_ge(act_free, s["qk"])
                    for m, job in enumerate(s["jobs"]):
                        banks_free(job)
                        r = slice(m * DHD, (m + 1) * DHD)
                        pe.matmul(ps[:, job.banks[0], 0:P], dqT[r, h, 0:P], dkT[r, h, 0:P], start=True, stop=True, skip_group_check=True)
                        pe.matmul(ps[:, job.banks[0], P:P + SEQ], dqT[r, h, P:2 * P], dkT[r, h, :], start=True, stop=True,
                                  skip_group_check=True).then_inc(job_done, 1)
                elif k == "d_out":
                    h, (jt, jo) = s["h"], s["jobs"]
                    banks_free(jt)
                    pe.wait_ge(d_a, h + 1)
                    a = dS[:, h % 2, 0, :]
                    pe.transpose(ps[:, jt.banks[0], 0:P], a[:, 0:P], ident)
                    pe.transpose(ps[:, jt.banks[0], P:2 * P], a[:, P:2 * P], ident)
                    pe.transpose(ps[:, jt.banks[0], 2 * P:3 * P], a[:, 2 * P:3 * P], ident).then_inc(job_done, 1)
                    banks_free(jo)
                    pe.wait_ge(act_free, jt.act)
                    c = slice(h * P, (h + 1) * P)
                    b = jo.banks[0]
                    pe.matmul(ps[:, b, 0:P], daT[:, 0:P], dv[:, 0, c], start=True, stop=True, skip_group_check=True)
                    pe.matmul(ps[:, b, P:2 * P], daT[:, P:2 * P], dv[:, 0, c], start=True, stop=False, skip_group_check=True)
                    pe.matmul(ps[:, b, P:2 * P], daT[:, 2 * P:3 * P], dv[:, 1, c], start=False, stop=True,
                              skip_group_check=True).then_inc(job_done, 1)
                elif k == "sgu_mix":
                    pe.wait_ge(sg_w, 1)
                    pe.wait_ge(sg_v, 1)
                    for m, job in enumerate(s["jobs"]):
                        t, half = divmod(m, 2)
                        banks_free(job)
                        for q in range(4):
                            g = 4 * half + q
                            mm = pe.matmul(ps[:, job.banks[0], q * P:(q + 1) * P], wsT[:, g, :],
                                           mix[:, t, D + g * P:D + (g + 1) * P], start=True, stop=True, skip_group_check=True)
                        mm.then_inc(job_done, 1)
                elif k == "x_score":
                    banks_free(s["job"])
                    pe.wait_ge(act_free, s["kv_q"])
                    for t in range(TT):
                        for c in range(2):
                            mm = pe.matmul(ps[:, s["job"].banks[0], t * MEM:(t + 1) * MEM], qT[:, 2 * s["h"] + c, t * P:(t + 1) * P],
                                           kT[:, 2 * s["h"] + c, :], start=c == 0, stop=c == 1, skip_group_check=True)
                    mm.then_inc(job_done, 1)
                elif k == "x_turn":
                    banks_free(s["job"])
                    pe.wait_ge(x_pn, s["n"] + 1)
                    p = xp[:, s["n"] % 2, :]
                    for c in range(2):
                        for t in range(TT):
                            mm = pe.transpose(ps[:, s["job"].banks[0], c * SEQ + t * P:c * SEQ + (t + 1) * P],
                                              p[:, t * MEM + c * P:t * MEM + (c + 1) * P], ident)
                    mm.then_inc(job_done, 1)
                elif k == "x_out":
                    banks_free(s["job"])
                    pe.wait_ge(act_free, s["pT"])
                    pT = xpT[:, s["n"] % 2, :]
                    for c in range(2):
                        for mt in range(2):
                            e0 = s["h"] * XD + c * P
                            mm = pe.matmul(ps[:, s["job"].banks[0], c * SEQ:(c + 1) * SEQ], v[:, mt, e0:e0 + P],
                                           pT[:, mt * SEQ:(mt + 1) * SEQ], start=mt == 0, stop=mt == 1, skip_group_check=True)
                    mm.then_inc(job_done, 1)
                elif k == "out":
                    banks_free(s["job"])
                    pe.wait_ge(act_free, split_jobs["act"].act)
                    pe.wait_ge(dve_free, split_jobs["act"].dve)
                    nu = len(s["us"])
                    natural(lambda n, t: 2 * t + n % 2, actT, s["src"], s["us"], lambda n: n < 2, lambda n: n >= nu - 2)
                elif k == "down":
                    if s["first"]:
                        banks_free(s["job"])
                    pe.wait_ge(ff_hi, s["nf"])
                    pe.wait_ge(ff_lo, s["nf"])
                    k0 = [(4 * s["b"] + c) % 24 for c in (0, 0, 2, 2)]
                    natural(lambda n, t: 2 * t + n % 2, actT, k0, s["us"], lambda n: s["first"] and n < 2, lambda n: s["last"] and n >= 2)

        @block.scalar
        def _(act):
            links = [0]
            split = [0]
            convs = [0]

            def link(ins):
                links[0] += 1
                ins.then_inc(act_chain, 1)
                act.wait_ge(act_chain, links[0])

            def split_to(n):
                while split[0] < min(n, NU):
                    u = split[0]
                    act.wait_ge(raw_in[u % RING], 16 * (u // RING + 1))
                    if u >= RING:
                        kind, value = plan.release[u - RING]
                        act.wait_ge(w_used if kind == "used" else job_done, value)
                        act.wait_ge(w_lo, u - RING + 1)
                    act.activation(w_hi_t[:, u % RING, :], raw[:, u % RING, :], ACT.Copy).then_inc(w_hi, 1)
                    split[0] += 1

            act.wait_ge(loaded, 64)
            for s in steps:
                k = s["kind"]
                split_to((s["us"][-1] + 1 if "us" in s else s["w"]) + RING)
                if k == "layer" and s["mixer"] == SGU:
                    act.wait_ge(ff_lo, s["ff"])
                    act.dma_start(wsT[:, :, :], A["sgu_wT"]).then_inc(sg_in, 16)
                    act.dma_start(sgain[:, :], A["sgu_gain"].partition_broadcast(P)).then_inc(sg_in, 16)
                elif k == "layer" and s["mixer"] == DIFF:
                    act.wait_ge(setup_done, 1)
                    act.activation(lam, lam, ACT.Exp).then_inc(expa_done, 1)
                elif k == "layer":
                    act.activation(expa[:, :], rw[:, RW["a_log"] + SH * s["l"]:RW["a_log"] + SH * (s["l"] + 1)], ACT.Exp).then_inc(expa_done, 1)
                elif k == "norm":
                    src = x if s["what"] == "x" else mix[:, :, D:2 * D]
                    if s["what"] == "x":
                        act.wait_ge(loaded2, 16)
                        if s["x_dve"]:
                            act.wait_ge(dve_free, s["x_dve"])
                    for t in range(TT):
                        ins = act.activation(mix[:, t, 0:D], src[:, t, :], ACT.Square, accum_out=ss[:, t:t + 1])
                    ins.then_inc(sumsq, 1)
                elif k == "split_turn":
                    hi = T[s["dst"]][0]
                    for m, job in enumerate(s["jobs"]):
                        act.wait_ge(job_done, job.done)
                        g = gains(s, m)
                        b = job.banks[0]
                        t0 = 2 * m
                        for f in range(2):
                            ins = act.activation(hi[:, t0 + f, :], ps[:, b, f * SEQ:(f + 1) * SEQ], ACT.Copy, scale=g[f] if g else 1.0)
                        ins.then_inc(act_free, 1)
                elif k == "turn":
                    dst = {"kT": kT, "qT": qT, "dq": dqT, "dk": dkT}[s["dst"]]
                    for m, job in enumerate(s["jobs"]):
                        act.wait_ge(job_done, job.done)
                        g = turn_gains(s, m)
                        for f in range(2):
                            ins = act.activation(dst[:, s["tile"] + 2 * m + f, :], ps[:, job.banks[0], f * SEQ:(f + 1) * SEQ], ACT.Copy, scale=g[f])
                        ins.then_inc(act_free, 1)
                elif k == "evac":
                    job, e = s["job"], s["evac"]
                    b0 = job.banks[0]
                    if job.act:
                        act.wait_ge(job_done, job.done)
                    if e == "norm":
                        for t in range(TT):
                            ins = act.activation(nt[:, t, :], ps[:, b0 + t, :], ACT.Square)
                        ins.then_inc(act_free, 1)
                    elif e in ("v", "dv"):
                        dst = v if e == "v" else dv
                        for t in range(TT):
                            ins = act.activation(dst[:, t, s["nb"] * COLS:(s["nb"] + 1) * COLS], ps[:, b0 + t, :], ACT.Copy)
                        ins.then_inc(act_free, 1)
                    elif e in ("z", "gelu"):
                        f = ACT.Silu if e == "z" else ACT.Gelu
                        for t in range(TT):
                            ins = act.activation(mix[:, t, s["nb"] * COLS:(s["nb"] + 1) * COLS], ps[:, b0 + t, :], f)
                        ins.then_inc(act_free, 1)
                    elif e == "conv":
                        dst = xsT if s["ft"] < 16 else bcT[:, s["ft"] - 16:s["ft"] - 12, :]
                        for f in range(4):
                            c = s["l"] * TAPS * 32 + 3 * 32 + s["ft"] + f
                            ins = act.activation(dst[:, f, :], ps[:, b0 + f // 2, (f % 2) * SEQ:(f % 2 + 1) * SEQ], ACT.Identity,
                                                 bias=col("conv_b", s["l"] * 32 + s["ft"] + f), scale=col("conv_w", c))
                        ins.then_inc(act_free, 1)
                    elif e == "relu2":
                        r = rf[s["nf"] % 2]
                        if s["nf"] > 2:
                            act.wait_ge(ff_lo, s["nf"] - 2)
                        act.activation(r[:, 0:512], ps[:, b0, :], ACT.Relu)
                        act.activation(r[:, 512:1024], ps[:, b0 + 1, :], ACT.Relu).then_inc(act_free, 1)
                        act.wait_ge(ff_f, s["nf"])
                        t0 = 4 * s["b"] % 24
                        act.activation(act_hi[:, t0:t0 + 4, :].rearrange("p a b -> p (a b)"), r[:, :], ACT.Copy).then_inc(ff_hi, 1)
                elif k == "silu":
                    dst = xsT[:, :, :] if s["ft"] < 16 else bcT[:, s["ft"] - 16:s["ft"] - 12, :]
                    act.wait_ge(dve_free, s["job"].dve)
                    act.activation(dst, dst, ACT.Silu).then_inc(conv_out, 1)
                elif k == "dt_turn":
                    act.wait_ge(dt_abs, s["n"])
                    act.activation(dts[1], dts[0], ACT.Exp, scale=-1.0).then_inc(dt_exp, 1)
                elif k == "decay":
                    act.wait_ge(job_done, s["job"].done)
                    act.activation(decay[:, :], ps[:, s["job"].banks[0], 0:2 * SH], ACT.Exp).then_inc(act_free, 1)
                elif k == "xs_turn":
                    for t, job in enumerate(s["jobs"]):
                        act.wait_ge(job_done, job.done)
                        act.activation(xs[:, t, s["k"] * COLS:(s["k"] + 1) * COLS], ps[:, job.banks[0], :], ACT.Copy).then_inc(act_free, 1)
                elif k == "ssd_a":
                    for b in range(TT):
                        job = s["jobs"]["S", b]
                        act.wait_ge(job_done, job.done)
                        act.activation(E[:, b, :], ps[:, job.banks[0], :], ACT.Exp).then_inc(act_free, 1)
                    act.wait_ge(job_done, s["jobs"]["B"].done)
                    act.activation(Bn[:, :], ps[:, s["jobs"]["B"].banks[0], 0:P], ACT.Copy).then_inc(act_free, 1)
                elif k == "ssd_b":
                    job = s["jobs"]["H"]
                    act.wait_ge(job_done, job.done)
                    act.activation(hst[:, :], ps[:, job.banks[0], 0:GW], ACT.Copy).then_inc(act_free, 1)
                elif k == "yg_square":
                    act.wait_ge(yg_new, s["n"] + 1)
                    for t in range(TT):
                        ins = act.activation(junk[:, :], mix[:, t, s["g"] * GW:(s["g"] + 1) * GW], ACT.Square,
                                             accum_out=ssy[:, t * SG + s["g"]:t * SG + s["g"] + 1])
                        if t == 0:
                            link(ins)
                    ins.then_inc(yg_sq, 1)
                    act.wait_ge(yg_sq, s["n"] + 1)
                elif k == "d_out":
                    jt, jo = s["jobs"]
                    h = s["h"]
                    act.wait_ge(job_done, jt.done)
                    act.activation(daT[:, :], ps[:, jt.banks[0], 0:384], ACT.Copy).then_inc(act_free, 1)
                    act.wait_ge(job_done, jo.done)
                    act.activation(mix[:, :, h * P:(h + 1) * P], ps[:, jo.banks[0], 0:SEQ].rearrange("p (t n) -> p t n", t=TT),
                                   ACT.Copy).then_inc(act_free, 1)
                elif k == "d_score":
                    h = s["h"]
                    act.wait_ge(d_nb, h + 1)
                    for m in range(2):
                        for t in range(TT):
                            a = dS[:, h % 2, m, 0:P] if t == 0 else dS[:, h % 2, m, P:384]
                            q = 2 * m + t
                            ins = act.activation(a, a, ACT.Exp, bias=dnb[:, 4 * (h % 2) + q:4 * (h % 2) + q + 1],
                                                 accum_out=dsm[:, 4 * (h % 2) + q:4 * (h % 2) + q + 1])
                    ins.then_inc(d_p, 1)
                elif k == "x_score":
                    n = s["n"]
                    act.wait_ge(dve_free, s["job"].dve)
                    for t in range(TT):
                        q = 2 * (n % 2) + t
                        ins = act.activation(xp[:, n % 2, t * MEM:(t + 1) * MEM], ps[:, s["job"].banks[0], t * MEM:(t + 1) * MEM], ACT.Exp,
                                             bias=xnb[:, q:q + 1], accum_out=xsum[:, q:q + 1])
                    ins.then_inc(act_free, 1)
                elif k == "x_turn":
                    act.wait_ge(job_done, s["job"].done)
                    act.activation(xpT[:, s["n"] % 2, :], ps[:, s["job"].banks[0], :], ACT.Copy).then_inc(act_free, 1)
                elif k == "x_out":
                    act.wait_ge(job_done, s["job"].done)
                    t0 = CROSS0 + 2 * s["h"]
                    act.activation(act_hi[:, t0:t0 + 2, :].rearrange("p a b -> p (a b)"), ps[:, s["job"].banks[0], :], ACT.Copy).then_inc(act_free, 1)
            split_to(NU)

        @block.vector
        def _(dve):
            links = [0]

            def link(ins):
                links[0] += 1
                ins.then_inc(dve_chain, 1)
                dve.wait_ge(dve_chain, links[0])

            def rsqrt(y, total, width):
                n = total.shape[-1]
                m, b = ta[:, 0:n], tb[:, 0:n]
                link(dve.tensor_scalar(m, total, 1.0 / width, EPS, ALU.mult, ALU.add))
                link(dve.tensor_scalar(b.bitcast(I32), m.bitcast(I32), 1, None, ALU.logical_shift_right))
                link(dve.tensor_scalar(y.bitcast(I32), b.bitcast(I32), -1.0, RSQRT_SEED, ALU.mult, ALU.add))
                for _ in range(3):
                    link(dve.tensor_tensor(b, m, y, ALU.mult))
                    link(dve.scalar_tensor_tensor(out=b, in0=b, scalar=-0.5, in1=y, op0=ALU.mult, op1=ALU.mult))
                    link(dve.scalar_tensor_tensor(out=y, in0=b, scalar=1.5, in1=y, op0=ALU.add, op1=ALU.mult))

            def over(a, groups, width):
                return a.unsqueeze(2).to_broadcast([P, groups, width])

            def heads(a, n=HPG):
                return a.rearrange("p (h c) -> p h c", h=n)

            dve.wait_ge(loaded, 64)
            link(dve.tensor_scalar(gq8, col("dq"), DHD ** -0.5, None, ALU.mult))
            link(dve.tensor_scalar(gx16[:, :], pc[:, PC["xq"]:PC["xq"] + 8], XD ** -0.5, None, ALU.mult))
            link(dve.tensor_scalar(gsub, col("dsub"), 1.0 - LAMBDA_INIT, None, ALU.mult))
            for m in range(2):
                a, b = RW["lq%d" % (m + 1)], RW["lk%d" % (m + 1)]
                link(dve.tensor_tensor(rw[:, a:a + 64], rw[:, a:a + 64], rw[:, b:b + 64], ALU.mult))
                ins = dve.tensor_reduce(lam[:, m:m + 1], rw[:, a:a + 64], AX.X, ALU.add)
                if m == 0:
                    link(ins)
            ins.then_inc(setup_done, 1)
            lam_ready = False
            for s in steps:
                k = s["kind"]
                if k == "layer" and s["mixer"] == DIFF:
                    dve.wait_ge(expa_done, 2)
                    link(dve.tensor_tensor(lam2, lam[:, 1:2], lam[:, 0:1], ALU.subtract))
                    link(dve.tensor_scalar(lam2, lam2, -LAMBDA_INIT, None, ALU.add))
                elif k == "norm":
                    dve.wait_ge(sumsq, s["n"])
                    rsqrt(r_x, ss, D)
                    src = x if s["what"] == "x" else mix[:, :, D:2 * D]
                    for t in range(TT):
                        ins = dve.tensor_scalar(mix[:, t, 0:D], src[:, t, :], r_x[:, t:t + 1], None, ALU.mult)
                    ins.then_inc(xn_new, 1)
                elif k == "split_turn":
                    hi, lo = T[s["dst"]]
                    for m, job in enumerate(s["jobs"]):
                        dve.wait_ge(act_free, job.act)
                        g = gains(s, m)
                        b = job.banks[0]
                        t0 = 2 * m
                        if g is None:
                            ins = dve.tensor_tensor(lo[:, t0:t0 + 2, :].rearrange("p a b -> p (a b)"), ps[:, b, :],
                                                    hi[:, t0:t0 + 2, :].rearrange("p a b -> p (a b)").bitcast(F32), ALU.subtract)
                        else:
                            for f in range(2):
                                ins = dve.scalar_tensor_tensor(out=lo[:, t0 + f, :], in0=ps[:, b, f * SEQ:(f + 1) * SEQ], scalar=g[f],
                                                               in1=hi[:, t0 + f, :].bitcast(F32), op0=ALU.mult, op1=ALU.subtract)
                        ins.then_inc(dve_free, 1)
                elif k == "evac":
                    job, e = s["job"], s["evac"]
                    b0 = job.banks[0]
                    if e == "norm":
                        ng = s["groups"]
                        dve.wait_ge(act_free, job.act)
                        link(dve.tensor_reduce(ssn[:, 0:TT * ng], nt[:, :, :].rearrange("p t (g c) -> p (t g) c", g=ng), AX.X, ALU.add))
                        rsqrt(r_nt[:, 0:TT * ng], ssn[:, 0:TT * ng], COLS // ng)
                        for t in range(TT):
                            ins = dve.tensor_tensor(heads(nt[:, t, :], ng), heads(ps[:, b0 + t, :], ng),
                                                    over(r_nt[:, t * ng:(t + 1) * ng], ng, COLS // ng), ALU.mult)
                        ins.then_inc(dve_free, 1)
                    elif e == "conv":
                        dst = xsT if s["ft"] < 16 else bcT[:, s["ft"] - 16:s["ft"] - 12, :]
                        dve.wait_ge(act_free, job.act)
                        for d in range(1, TAPS):
                            for f in range(4):
                                c = s["l"] * TAPS * 32 + (TAPS - 1 - d) * 32 + s["ft"] + f
                                ins = dve.scalar_tensor_tensor(out=dst[:, f, d:SEQ], in0=ps[:, b0 + f // 2, (f % 2) * SEQ:(f % 2 + 1) * SEQ - d],
                                                               scalar=col("conv_w", c), in1=dst[:, f, d:SEQ], op0=ALU.mult, op1=ALU.add)
                                if d < TAPS - 1 and f == 3:
                                    link(ins)
                        ins.then_inc(dve_free, 1)
                    elif e == "dt":
                        dve.wait_ge(job_done, job.done)
                        dve.tensor_copy(dtT[0:SH, :], ps[0:SH, b0, 0:SEQ]).then_inc(dve_free, 1)
                    elif e == "relu2":
                        r = rf[s["nf"] % 2]
                        dve.wait_ge(act_free, job.act)
                        dve.tensor_tensor(r[:, :], r[:, :], r[:, :], ALU.mult).then_inc(ff_f, 1)
                        dve.wait_ge(ff_hi, s["nf"])
                        t0 = 4 * s["b"] % 24
                        dve.tensor_tensor(act_lo[:, t0:t0 + 4, :].rearrange("p a b -> p (a b)"), r[:, :],
                                          act_hi[:, t0:t0 + 4, :].rearrange("p a b -> p (a b)").bitcast(F32), ALU.subtract).then_inc(ff_lo, 1)
                elif k == "dt_turn":
                    dve.wait_ge(job_done, s["job"].done)
                    dve.wait_ge(act_free, s["nt_free"])
                    raw_dt, ee, den, z, z2, acc, big = dts[0], dts[1], dts[2], dts[3], dts[4], dts[5], dts[6]
                    bias = rw[:, RW["dt_bias"] + SH * s["l"]:RW["dt_bias"] + SH * (s["l"] + 1)].unsqueeze(1).to_broadcast([P, TT, SH])
                    dve.tensor_tensor(heads(acc, TT), heads(ps[:, s["job"].banks[0], 0:2 * SH], TT), bias, ALU.add).then_inc(dve_free, 1)
                    dve.wait_ge(dve_free, s["job"].dve)
                    link(dve.tensor_scalar(big, acc, 0.0, None, ALU.max))
                    dve.scalar_tensor_tensor(out=raw_dt, in0=acc, scalar=-1.0, in1=acc, op0=ALU.mult, op1=ALU.max).then_inc(dt_abs, 1)
                    dve.wait_ge(dt_exp, s["n"])
                    link(dve.tensor_scalar(den, ee, 2.0, None, ALU.add))
                    link(dve.reciprocal(den, den))
                    link(dve.tensor_tensor(z, ee, den, ALU.mult))
                    link(dve.tensor_tensor(z2, z, z, ALU.mult))
                    link(dve.tensor_scalar(acc, z2, 1.0 / 17, None, ALU.mult))
                    for o in (15, 13, 11, 9, 7, 5, 3):
                        link(dve.scalar_tensor_tensor(out=acc, in0=acc, scalar=1.0 / o, in1=z2, op0=ALU.add, op1=ALU.mult))
                    link(dve.scalar_tensor_tensor(out=acc, in0=acc, scalar=1.0, in1=z, op0=ALU.add, op1=ALU.mult))
                    link(dve.scalar_tensor_tensor(out=dt_v, in0=acc, scalar=2.0, in1=big, op0=ALU.mult, op1=ALU.add))
                    dve.wait_ge(expa_done, 1 if s["l"] == 0 else 3)
                    ea = expa[:, :].unsqueeze(1).to_broadcast([P, TT, SH])
                    dve.scalar_tensor_tensor(out=heads(adt, TT), in0=heads(dt_v, TT), scalar=-1.0, in1=ea, op0=ALU.mult, op1=ALU.mult)\
                        .then_inc(adt_new, 1)
                    dve.wait_ge(adt_new, s["n"])
                elif k == "ssd_mv":
                    g = s["g"]
                    for b in range(TT):
                        a = adt[:, b * SH + HPG * g:b * SH + HPG * (g + 1)]
                        ins = dve.tensor_tensor(heads(mv[:, b, :]), upto.unsqueeze(1).to_broadcast([P, HPG, P]), over(a, HPG, P), ALU.mult)
                    ins.then_inc(mv_new, 1)
                elif k == "ssd_a":
                    g, n = s["g"], s["n"]
                    dve.wait_ge(act_free, s["xs"])
                    for b in range(TT):
                        a = dt_v[:, b * SH + HPG * g:b * SH + HPG * (g + 1)]
                        if b == 0:
                            link(dve.tensor_tensor(heads(xdt[:, b, :]), heads(xs[:, b, g * GW:(g + 1) * GW]), over(a, HPG, SHD), ALU.mult))
                        else:
                            dve.tensor_tensor(heads(xdt[:, b, :]), heads(xs[:, b, g * GW:(g + 1) * GW]), over(a, HPG, SHD), ALU.mult)
                    dve.tensor_tensor(heads(xw[:, :]), heads(xdt[:, 0, :]), over(decay[:, HPG * g:HPG * (g + 1)], HPG, SHD), ALU.mult)\
                        .then_inc(xdt_new, 1)
                    dve.wait_ge(xdt_new, n + 1)
                    d = rw[:, RW["ssm_d"] + SH * s["l"] + HPG * g:RW["ssm_d"] + SH * s["l"] + HPG * (g + 1)]
                    for b in range(TT):
                        c = xs[:, b, g * GW:(g + 1) * GW]
                        ins = dve.tensor_tensor(heads(c), heads(c), over(d, HPG, SHD), ALU.mult)
                    link(ins)
                    for b in range(TT):
                        jc, js = s["jobs"]["C", b], s["jobs"]["S", b]
                        dve.wait_ge(job_done, jc.done)
                        dve.tensor_tensor(cbm[:, b, :], ps[:, jc.banks[0], 0:P], upto, ALU.mult).then_inc(dve_free, 1)
                        dve.wait_ge(dve_free, jc.dve)
                        dve.wait_ge(act_free, js.act)
                        dve.tensor_tensor(heads(E[:, b, :]), heads(E[:, b, :]), cbm[:, b, :].unsqueeze(1).to_broadcast([P, HPG, P]), ALU.mult)\
                            .then_inc(m_new, 1)
                elif k == "ssd_b":
                    g, n, jobs = s["g"], s["n"], s["jobs"]
                    for b in range(TT):
                        c = xs[:, b, g * GW:(g + 1) * GW]
                        job = jobs["Y", b]
                        dve.wait_ge(job_done, job.done)
                        y = ps[:, job.banks[0], :].rearrange("p (h c) -> p h c", h=HPG)[:, :, 0:SHD]
                        dve.tensor_tensor(heads(c), y, heads(c), ALU.add).then_inc(dve_free, 1)
                        dve.wait_ge(dve_free, job.dve)
                    job = jobs["O"]
                    dve.wait_ge(job_done, job.done)
                    dve.tensor_tensor(heads(xw[:, :]), heads(ps[:, job.banks[0], 0:GW]),
                                      over(decay[:, SH + HPG * g:SH + HPG * (g + 1)], HPG, SHD), ALU.mult).then_inc(dve_free, 1)
                    dve.wait_ge(dve_free, job.dve)
                    c = xs[:, 1, g * GW:(g + 1) * GW]
                    link(dve.tensor_tensor(c, c, xw[:, :], ALU.add))
                    for b in range(TT):
                        c, m = xs[:, b, g * GW:(g + 1) * GW], mix[:, b, g * GW:(g + 1) * GW]
                        ins = dve.tensor_tensor(m, m, c, ALU.mult)
                    ins.then_inc(yg_new, 1)
                elif k == "group_norm":
                    if s["what"] == SSM:
                        dve.wait_ge(yg_sq, SG * (s["l"] + 1))
                        rsqrt(r_y, ssy, GW)
                        for t in range(TT):
                            m = heads(mix[:, t, :], SG)
                            ins = dve.tensor_tensor(m, m, over(r_y[:, t * SG:(t + 1) * SG], SG, GW), ALU.mult)
                    else:
                        dve.wait_ge(act_free, s["o_act"])
                        dsq = dS[:, :, :, :].rearrange("p a b c -> p (a b c)")[:, 0:D]
                        for t in range(TT):
                            link(dve.tensor_tensor(dsq, mix[:, t, 0:D], mix[:, t, 0:D], ALU.mult))
                            link(dve.tensor_reduce(ssy[:, t * DH:(t + 1) * DH], heads(dsq, DH), AX.X, ALU.add))
                        rsqrt(r_y, ssy, 2 * DHD)
                        for t in range(TT):
                            m = heads(mix[:, t, 0:D], DH)
                            ins = dve.tensor_tensor(m, m, over(r_y[:, t * DH:(t + 1) * DH], DH, P), ALU.mult)
                    ins.then_inc(mix_new, 1)
                elif k == "d_score":
                    h = s["h"]
                    for m, job in enumerate(s["jobs"]):
                        dve.wait_ge(job_done, job.done)
                        ins = dve.scalar_tensor_tensor(out=dS[:, h % 2, m, :], in0=dist, scalar=2.0 ** -(h + 1), in1=ps[:, job.banks[0], 0:384],
                                                       op0=ALU.mult, op1=ALU.add)
                        ins.then_inc(dve_free, 1)
                        dve.wait_ge(dve_free, job.dve)
                    q = 4 * (h % 2)
                    for m in range(2):
                        dve.tensor_reduce(dnb[:, q + 2 * m:q + 2 * m + 1], dS[:, h % 2, m, 0:P], AX.X, ALU.max, negate=True)
                        ins = dve.tensor_reduce(dnb[:, q + 2 * m + 1:q + 2 * m + 2], dS[:, h % 2, m, P:384], AX.X, ALU.max, negate=True)
                    ins.then_inc(d_nb, 1)
                    dve.wait_ge(d_p, h + 1)
                    link(dve.reciprocal(drs[:, :], dsm[:, q:q + 4]))
                    link(dve.tensor_scalar(drs[:, 2:4], drs[:, 2:4], lam2, None, ALU.mult))
                    a0, a1 = dS[:, h % 2, 0, :], dS[:, h % 2, 1, :]
                    parts = [(0, slice(0, P)), (1, slice(P, 384))]
                    for t, c in parts:
                        ins = dve.tensor_scalar(a1[:, c], a1[:, c], drs[:, 2 + t:3 + t], None, ALU.mult)
                    link(ins)
                    for t, c in parts:
                        ins = dve.scalar_tensor_tensor(out=a0[:, c], in0=a0[:, c], scalar=drs[:, t:t + 1], in1=a1[:, c], op0=ALU.mult, op1=ALU.add)
                    ins.then_inc(d_a, 1)
                elif k == "sgu_norm":
                    dve.wait_ge(sg_in, 32)
                    dve.tensor_tensor(wsT[:, :, :], wsT[:, :, :], sgu_mask.unsqueeze(1).to_broadcast([P, SGG, P]), ALU.mult).then_inc(sg_w, 1)
                    dve.wait_ge(act_free, s["v_act"])
                    for t in range(TT):
                        vv = mix[:, t, D:2 * D]
                        sq = qT[:, 0:4, :].rearrange("p a b -> p (a b)")
                        link(dve.tensor_tensor(sq, vv, vv, ALU.mult))
                        link(dve.tensor_reduce(ssy[:, t * SGG:(t + 1) * SGG], heads(sq, SGG), AX.X, ALU.add))
                    rsqrt(r_y, ssy, SGW)
                    for t in range(TT):
                        vv = mix[:, t, D:2 * D]
                        link(dve.tensor_tensor(heads(vv, SGG), heads(vv, SGG), over(r_y[:, t * SGG:(t + 1) * SGG], SGG, SGW), ALU.mult))
                        ins = dve.tensor_tensor(vv, vv, sgain[:, :], ALU.mult)
                        if t == 0:
                            link(ins)
                    ins.then_inc(sg_v, 1)
                elif k == "sgu_mix":
                    dve.wait_ge(act_free, s["u_act"])
                    for m, job in enumerate(s["jobs"]):
                        t, half = divmod(m, 2)
                        dve.wait_ge(job_done, job.done)
                        for q in range(4):
                            g = 4 * half + q
                            u = mix[:, t, g * P:(g + 1) * P]
                            ins = dve.scalar_tensor_tensor(out=u, in0=ps[:, job.banks[0], q * P:(q + 1) * P], scalar=col("b_s", g), in1=u,
                                                           op0=ALU.add, op1=ALU.mult)
                        ins.then_inc(dve_free, 1)
                elif k == "x_score":
                    n = s["n"]
                    dve.wait_ge(job_done, s["job"].done)
                    q = 2 * (n % 2)
                    dve.tensor_reduce(xnb[:, q:q + 2], ps[:, s["job"].banks[0], :].rearrange("p (t m) -> p t m", t=TT), AX.X, ALU.max,
                                      negate=True).then_inc(dve_free, 1)
                    dve.wait_ge(act_free, s["job"].act)
                    link(dve.reciprocal(xrs[:, :], xsum[:, q:q + 2]))
                    for t in range(TT):
                        p = xp[:, n % 2, t * MEM:(t + 1) * MEM]
                        ins = dve.tensor_scalar(p, p, xrs[:, t:t + 1], None, ALU.mult)
                    ins.then_inc(x_pn, 1)
                elif k == "x_out":
                    dve.wait_ge(act_free, s["job"].act)
                    t0 = CROSS0 + 2 * s["h"]
                    dve.tensor_tensor(act_lo[:, t0:t0 + 2, :].rearrange("p a b -> p (a b)"), ps[:, s["job"].banks[0], :],
                                      act_hi[:, t0:t0 + 2, :].rearrange("p a b -> p (a b)").bitcast(F32), ALU.subtract).then_inc(dve_free, 1)
                elif k == "out" or (k == "down" and s["last"]):
                    dve.wait_ge(job_done, s["job"].done)
                    for t in range(TT):
                        for nb in range(2):
                            c = x[:, t, nb * COLS:(nb + 1) * COLS]
                            ins = dve.tensor_tensor(c, ps[:, 2 * t + nb, :], c, ALU.add)
                    ins.then_inc(dve_free, 1)
                    dve.wait_ge(dve_free, s["job"].dve)


def columns(a):
    return np.ascontiguousarray(a.reshape(-1, P).T)


def constants():
    c = np.zeros((P, NCN), np.float32)
    k, n = np.arange(P)[:, None], np.arange(P)[None, :]
    c[:, CN["ident"]:CN["ident"] + P] = k == n
    c[:, CN["upto"]:CN["upto"] + P] = k <= n
    c[:, CN["after"]:CN["after"] + P] = k > n
    at = CN["dist"]
    for t in range(TT):
        q, keys = k + t * P, np.arange((t + 1) * P)[None, :]
        c[:, at:at + (t + 1) * P] = np.where(keys // 64 <= q // 64, -np.abs(q - keys).astype(np.float32), np.float32(-1e30))
        at += (t + 1) * P
    c[:, CN["sgu_mask"]:CN["sgu_mask"] + P] = k // 64 <= n // 64
    return c


def kernel(**inputs):
    import concourse.bacc as _bacc
    from concourse.bass_utils import run_bass_kernel_spmd as _run

    a = {k: np.asarray(v) for k, v in inputs.items()}
    units = Plan().units
    stream = np.empty((len(units), P, UNIT), np.float32)
    for u, (w, k, c) in enumerate(units):
        if w == "dt":
            first = DIN + XBC
            stream[u] = a["w_in_ssm"][k][:, first:first + P].reshape(8, P, P).transpose(1, 0, 2).reshape(P, UNIT)
        else:
            stream[u] = a[w[0]][w[1]][k * P:(k + UK) * P, c:c + COLS].reshape(UK, P, COLS).transpose(1, 0, 2).reshape(P, UNIT)
    percol = np.concatenate(
        [columns(a[n]) for n in ("norm_mix", "norm_ffn", "mem_norm", "xq_norm", "xk_norm", "ssm_conv_w", "ssm_conv_b", "ssm_gate_norm")]
        + [columns(np.concatenate([a[n], a[n]], axis=1)) for n in ("diff_q_norm", "diff_k_norm")]
        + [columns(a["diff_sub_norm"]), columns(a["sgu_b_s"])], axis=1)
    rows = np.concatenate([a[n].reshape(-1) for n in ("ssm_dt_bias", "ssm_a_log", "ssm_d", "diff_lq1", "diff_lk1", "diff_lq2", "diff_lk2")])
    arrays = {
        "x": a["x"], "mem": a["mem"], "wstream": stream, "percol": np.ascontiguousarray(percol), "rows": rows,
        "consts": constants(), "sgu_wT": np.ascontiguousarray(a["sgu_w_s"][0].transpose(2, 0, 1)), "sgu_gain": a["sgu_v_norm"].reshape(-1),
    }
    nc = _bacc.Bacc("TRN2", target_bir_lowering=False, num_devices=1)
    arrays = {"in_" + k: v for k, v in arrays.items()}
    aps = {k[3:]: nc.dram_tensor(k, v.shape, F32, kind="ExternalInput").ap() for k, v in arrays.items()}
    out = nc.dram_tensor("out_0", a["x"].shape, F32, kind="ExternalOutput").ap()
    bass_trunk(nc, aps, out)
    r = _run(nc, [arrays], core_ids=[0])
    return r.results[0]["out_0"]
```
